# Optimizing a Trainium2 kernel written in Bass

```python
import jax, jax.numpy as jnp
from jax import lax
import numpy as np

D_MODEL = 1024
BATCH = 1
SEQ = 256
DEPTH = 2

RET_HEADS = 8
RET_DK = 64
RET_DV = D_MODEL // RET_HEADS
RET_CHUNK = 128
RET_ROPE_BASE = 10000.0
ATT_HD = 64
ATT_HEADS = D_MODEL // ATT_HD
ATT_KV_HEADS = 4
WINDOW = 128
ATT_BLOCK = 128
ROPE_DIMS = ATT_HD // 4
ROPE_THETA = 500000.0
PEER_HEADS = 8
PEER_NKEYS = 128
PEER_EXPERTS = PEER_NKEYS * PEER_NKEYS
PEER_QDIM = 256
PEER_TOPK = 16
PEER_CHUNK = 128

EPS = 1e-6
NEG_INF = -1e30

kernel_name = "hybrid_retention_swa_peer_adaln"

def rmsnorm(x, g):
    xf = x.astype(jnp.float32)
    y = xf * lax.rsqrt(jnp.mean(xf * xf, axis=-1, keepdims=True) + EPS)
    return (y * g.astype(jnp.float32)).astype(x.dtype)

def rotary(t, positions, n_rot, base):
    half = n_rot // 2
    inv = jnp.power(base, -jnp.arange(half, dtype=jnp.float32) * (2.0 / n_rot))
    ang = positions.astype(jnp.float32)[..., None] * inv
    cos = jnp.cos(ang)[:, :, None, :].astype(t.dtype)
    sin = jnp.sin(ang)[:, :, None, :].astype(t.dtype)
    t1 = t[..., :half]
    t2 = t[..., half:n_rot]
    rot = jnp.concatenate([t1 * cos - t2 * sin, t2 * cos + t1 * sin], axis=-1)
    if n_rot == t.shape[-1]:
        return rot
    return jnp.concatenate([rot, t[..., n_rot:]], axis=-1)

def retention(q, k, v):
    B, S, H, dk = q.shape
    dv = v.shape[-1]
    C = RET_CHUNK
    N = S // C
    dt = q.dtype
    k = k * (dk ** -0.5)
    qc = q.reshape(B, N, C, H, dk)
    kc = k.reshape(B, N, C, H, dk)
    vc = v.reshape(B, N, C, H, dv)
    log_g = jnp.log(1.0 - jnp.power(2.0, -5.0 - jnp.arange(H, dtype=jnp.float32)))
    idx = jnp.arange(C, dtype=jnp.float32)
    diff = idx[:, None] - idx[None, :]
    decay = jnp.where(diff >= 0, jnp.exp(log_g[:, None, None] * jnp.maximum(diff, 0.0)), 0.0)
    scores = jnp.einsum('bnchd,bnmhd->bnhcm', qc, kc) * decay.astype(dt)
    inner = jnp.einsum('bnhcm,bnmhe->bnche', scores, vc)
    k_w = jnp.exp(log_g[:, None] * (C - 1.0 - idx)[None, :]).astype(dt)
    kv = jnp.einsum('bnmhd,bnmhe,hm->nbhde', kc, vc, k_w)
    chunk_decay = jnp.exp(log_g * C).astype(kv.dtype)[:, None, None]

    def step(state, kv_i):
        return state * chunk_decay + kv_i, state

    _, prev = lax.scan(step, jnp.zeros((B, H, dk, dv), kv.dtype), kv)
    q_w = jnp.exp(log_g[:, None] * (idx + 1.0)[None, :]).astype(dt)
    cross = jnp.einsum('bnchd,nbhde,hc->bnche', qc, prev, q_w)
    return (inner + cross).reshape(B, S, H, dv)

def head_groupnorm(o, g):
    B, S, H, dv = o.shape
    of = o.astype(jnp.float32)
    mu = jnp.mean(of, axis=-1, keepdims=True)
    var = jnp.mean(jnp.square(of - mu), axis=-1, keepdims=True)
    y = ((of - mu) * lax.rsqrt(var + EPS)).reshape(B, S, H * dv)
    return (y * g.astype(jnp.float32)).astype(o.dtype)

def sliding_window_attention(q, k, v, sinks):
    B, S, HQ, Dh = q.shape
    HKV = k.shape[2]
    G = HQ // HKV
    L = ATT_BLOCK
    N = S // L
    qb = (q * (Dh ** -0.5)).reshape(B, N, L, HKV, G, Dh)
    kb = k.reshape(B, N, L, HKV, Dh)
    vb = v.reshape(B, N, L, HKV, Dh)

    def with_prev(t):
        prev = jnp.concatenate([jnp.zeros_like(t[:, :1]), t[:, :-1]], axis=1)
        return jnp.concatenate([prev, t], axis=2)

    kk = with_prev(kb)
    vv = with_prev(vb)
    s = jnp.einsum('bnqhgd,bnkhd->bnhgqk', qb, kk).astype(jnp.float32)
    qi = jnp.arange(L)[:, None]
    ki = jnp.arange(2 * L)[None, :]
    rel = qi + L - ki
    kpos = jnp.arange(N)[:, None, None] * L - L + ki[None]
    valid = (rel >= 0)[None] & (rel < WINDOW)[None] & (kpos >= 0)
    s = jnp.where(valid[None, :, None, None], s, NEG_INF)
    sink = sinks.astype(jnp.float32).reshape(1, 1, HKV, G, 1, 1)
    m = jnp.maximum(jnp.max(s, axis=-1, keepdims=True), sink)
    p = jnp.exp(s - m)
    p = p / (jnp.sum(p, axis=-1, keepdims=True) + jnp.exp(sink - m))
    o = jnp.einsum('bnhgqk,bnkhd->bnqhgd', p.astype(v.dtype), vv)
    return o.reshape(B, S, HQ * Dh)

def token_mixer(h, positions, w_in, ret_gn_g, sinks, w_out):
    B, S, _ = h.shape
    widths = (RET_HEADS * RET_DK, RET_HEADS * RET_DK, RET_HEADS * RET_DV, RET_HEADS * RET_DV,
              ATT_HEADS * ATT_HD, ATT_KV_HEADS * ATT_HD, ATT_KV_HEADS * ATT_HD, D_MODEL, D_MODEL)
    cuts = [int(c) for c in np.cumsum(widths)[:-1]]
    proj = h @ w_in
    rq, rk, rv, rg, aq, ak, av, gate_a, gate_b = jnp.split(proj, cuts, axis=-1)
    rq = rotary(rq.reshape(B, S, RET_HEADS, RET_DK), positions, RET_DK, RET_ROPE_BASE)
    rk = rotary(rk.reshape(B, S, RET_HEADS, RET_DK), positions, RET_DK, RET_ROPE_BASE)
    ro = retention(rq, rk, rv.reshape(B, S, RET_HEADS, RET_DV))
    ya = head_groupnorm(ro, ret_gn_g) * jax.nn.silu(rg)
    aq = rotary(aq.reshape(B, S, ATT_HEADS, ATT_HD), positions, ROPE_DIMS, ROPE_THETA)
    ak = rotary(ak.reshape(B, S, ATT_KV_HEADS, ATT_HD), positions, ROPE_DIMS, ROPE_THETA)
    yb = sliding_window_attention(aq, ak, av.reshape(B, S, ATT_KV_HEADS, ATT_HD), sinks)
    merged = jax.nn.sigmoid(gate_a) * ya + jax.nn.sigmoid(gate_b) * yb
    return merged @ w_out

def peer(h, wq, k1, k2, u, v):
    B, S, D = h.shape
    H, K, half = PEER_HEADS, PEER_TOPK, PEER_QDIM // 2
    q = (h @ wq).reshape(B, S, H, PEER_QDIM)
    s1 = jnp.einsum('bshd,hnd->bshn', q[..., :half], k1).astype(jnp.float32)
    s2 = jnp.einsum('bshd,hnd->bshn', q[..., half:], k2).astype(jnp.float32)
    v1, i1 = lax.top_k(s1, K)
    v2, i2 = lax.top_k(s2, K)
    cand = (v1[..., :, None] + v2[..., None, :]).reshape(B, S, H, K * K)
    cand_idx = (i1[..., :, None] * PEER_NKEYS + i2[..., None, :]).reshape(B, S, H, K * K)
    top_s, pos = lax.top_k(cand, K)
    experts = jnp.take_along_axis(cand_idx, pos, axis=-1)
    gates = jax.nn.softmax(top_s, axis=-1).astype(h.dtype)
    n_chunk = (B * S) // PEER_CHUNK
    hx = h.reshape(n_chunk, PEER_CHUNK, D)
    ex = experts.reshape(n_chunk, PEER_CHUNK, H * K)
    gx = gates.reshape(n_chunk, PEER_CHUNK, H * K)

    def one_chunk(args):
        xc, ec, gc = args
        act = jax.nn.gelu(jnp.einsum('td,tkd->tk', xc, u[ec]), approximate=False)
        return jnp.einsum('tk,tkd->td', act * gc, v[ec])

    y = lax.map(one_chunk, (hx, ex, gx))
    return y.reshape(B, S, D)

def setup_inputs(seed: int = 0) -> dict:
    key = jax.random.key(seed)
    ks = jax.random.split(key, 18)
    D = D_MODEL
    in_w = 2 * RET_HEADS * RET_DK + 2 * RET_HEADS * RET_DV + ATT_HEADS * ATT_HD + 2 * ATT_KV_HEADS * ATT_HD + 2 * D
    nrm = jax.random.normal
    x = nrm(ks[0], (BATCH, SEQ, D), jnp.float32)
    c = nrm(ks[1], (BATCH, D), jnp.float32)
    positions = (jnp.arange(SEQ, dtype=jnp.int32)[None, :]
                 + jax.random.randint(ks[2], (BATCH, 1), 0, 1024, dtype=jnp.int32))
    ada_w = nrm(ks[3], (DEPTH, D, 6 * D), jnp.float32) * (0.2 * D ** -0.5)
    ada_b = nrm(ks[4], (DEPTH, 6 * D), jnp.float32) * 0.1
    norm1_g = 1.0 + 0.05 * nrm(ks[5], (DEPTH, D), jnp.float32)
    norm2_g = 1.0 + 0.05 * nrm(ks[6], (DEPTH, D), jnp.float32)
    w_in = nrm(ks[7], (DEPTH, D, in_w), jnp.float32) * D ** -0.5
    ret_gn_g = 1.0 + 0.05 * nrm(ks[8], (DEPTH, RET_HEADS * RET_DV), jnp.float32)
    sinks = 0.5 * nrm(ks[9], (DEPTH, ATT_HEADS), jnp.float32)
    w_out = nrm(ks[10], (DEPTH, D, D), jnp.float32) * D ** -0.5
    peer_wq = nrm(ks[11], (DEPTH, D, PEER_HEADS * PEER_QDIM), jnp.float32) * D ** -0.5
    peer_k1 = nrm(ks[12], (DEPTH, PEER_HEADS, PEER_NKEYS, PEER_QDIM // 2), jnp.float32) * (PEER_QDIM // 2) ** -0.5
    peer_k2 = nrm(ks[13], (DEPTH, PEER_HEADS, PEER_NKEYS, PEER_QDIM // 2), jnp.float32) * (PEER_QDIM // 2) ** -0.5
    peer_u = nrm(ks[14], (DEPTH, PEER_EXPERTS, D), jnp.float32) * D ** -0.5
    peer_v = nrm(ks[15], (DEPTH, PEER_EXPERTS, D), jnp.float32) * PEER_HEADS ** -0.5
    final_g = 1.0 + 0.05 * nrm(ks[16], (D,), jnp.float32)
    return {"x": x, "c": c, "positions": positions, "ada_w": ada_w, "ada_b": ada_b,
            "norm1_g": norm1_g, "norm2_g": norm2_g, "w_in": w_in, "ret_gn_g": ret_gn_g,
            "sinks": sinks, "w_out": w_out, "peer_wq": peer_wq, "peer_k1": peer_k1,
            "peer_k2": peer_k2, "peer_u": peer_u, "peer_v": peer_v, "final_g": final_g}

def reference(x, c, positions, ada_w, ada_b, norm1_g, norm2_g, w_in, ret_gn_g, sinks, w_out,
              peer_wq, peer_k1, peer_k2, peer_u, peer_v, final_g):
    cond = jax.nn.silu(c)
    for l in range(DEPTH):
        mod = cond @ ada_w[l] + ada_b[l]
        sh1, sc1, g1, sh2, sc2, g2 = jnp.split(mod, 6, axis=-1)
        h = rmsnorm(x, norm1_g[l]) * (1.0 + sc1[:, None]) + sh1[:, None]
        x = x + g1[:, None] * token_mixer(h, positions, w_in[l], ret_gn_g[l], sinks[l], w_out[l])
        h = rmsnorm(x, norm2_g[l]) * (1.0 + sc2[:, None]) + sh2[:, None]
        x = x + g2[:, None] * peer(h, peer_wq[l], peer_k1[l], peer_k2[l], peer_u[l], peer_v[l])
    return rmsnorm(x, final_g)


_drawn_inputs = setup_inputs


def setup_inputs(seed=0):
    import zlib

    import numpy as np

    out = dict(_drawn_inputs(seed))
    spreads = {}
    factors = {'norm1_g': 5.647, 'norm2_g': 5.557, 'ret_gn_g': 8.0, 'sinks': 32.762}
    for name, (base, spread) in spreads.items():
        noise = np.random.default_rng([zlib.crc32(name.encode()), seed]).standard_normal(out[name].shape)
        drawn = base * np.exp(spread * noise) if base else spread * noise
        out[name] = __import__('jax').numpy.asarray(drawn.astype(out[name].dtype))
    for name, factor in factors.items():
        out[name] = (out[name] * factor).astype(out[name].dtype)
    return out
```

```python
from contextlib import ExitStack

import concourse.bass as bass
import concourse.mybir as mybir
import numpy as np

F32 = mybir.dt.float32
F32R = mybir.dt.float32r
I32 = mybir.dt.int32
U32 = mybir.dt.uint32
ALU = mybir.AluOpType
ACT = mybir.ActivationFunctionType
AX_X = mybir.AxisListType.X
ds = bass.ds

P = 128
D = 1024
SEQ = 256
DEPTH = 2
EPS = 1e-6
KC = D // P
TB = SEQ // P
RH, RDK, RDV = 8, 64, 128
AH, AKV, AHD = 16, 4, 64
ATT_SCALE = AHD ** -0.5
PH, NKEYS, TOPK = 8, 128, 16
UNITS = TB * PH
REMOVED = -3.0e38

C_RQ, C_RK, C_AQ, C_AK, C_RV, C_AV, C_RG, C_GA, C_GB = 0, 4, 8, 16, 18, 26, 28, 36, 44
N_WIN = 52
N_ROT = C_RV // 2
N_WOUT, N_WQ, N_U, N_V = KC, 2 * PH, NKEYS, NKEYS
B_WIN = 0
B_WOUT = B_WIN + N_WIN
B_WQ = B_WOUT + N_WOUT
B_U = B_WQ + N_WQ
B_V = B_U + N_U
N_BLOCKS = B_V + N_V
RING = 4
N_MOD = 6 * KC
SH1, SC1, G1, SH2, SC2, G2 = range(0, N_MOD, KC)
MOD_FIRST = 2 * KC
MOD_SLOTS = 8
BATCH = 4
N_GATE = SEQ // BATCH

W_PJ = 0
W_SQ = W_PJ + N_WIN * SEQ
W_HF = W_SQ + KC * SEQ
W_DECAY = W_HF + KC * SEQ
DW = SEQ + P
W_TRIG = W_DECAY + RH * DW
W_MASK = W_TRIG + 4 * SEQ
W_VTOK = W_MASK + 2 * P
VW = D + AKV * AHD
W_S = 24576
W_PT = W_S + AH * 2 * P
W_DS = W_SQ
W_GN = W_DS + RH * DW
W_QT = 0
W_KT = W_DECAY
W_SCORE = 28672
W_STAGE = 26624
W_RES = W_STAGE - 3 * UNITS * TOPK
assert W_VTOK + TB * VW <= W_S and W_GN + 1024 <= W_DECAY
UNIT_BLOCKS = 6
N_U1 = UNIT_BLOCKS * UNITS
assert W_RES // SEQ >= N_U1

K_ID, K_ONE, K_IOTA, K_PR, K_PA = 0, 128, 256, 384, 512
K_FR, K_FA, K_EPS = 640, 641, 642
K_ALL = 643
V_N1, V_N2, V_GN, V_FIN = 0, 16, 32, 48
V_ADAB = 56
V_SINK = V_ADAB + DEPTH * N_MOD
V_ALL = V_SINK + DEPTH * AH

TWO_PI_1 = 6.28125
TWO_PI_2 = float(np.float32(2 * np.pi - 6.28125))
TWO_PI_3 = float(np.float32(2 * np.pi - 6.28125 - np.float64(np.float32(2 * np.pi - 6.28125))))
MAGIC = 12582912.0
PI_SAFE = 3.1415925


def ge(eng, sem, value):
    if isinstance(value, int) and value <= 0:
        return
    eng.wait_ge(sem, value)


class Steps:

    def __init__(self, eng, sem):
        self.eng, self.sem, self.n, self.shift = eng, sem, 0, 0

    def done(self, ins):
        ins.then_inc(self.sem, 1)
        self.n += 1
        return self.n + self.shift

    def wait(self, value=None):
        self.eng.wait_ge(self.sem, self.n + self.shift if value is None else value)

    def link(self, ins):
        self.done(ins)
        self.wait()

    def loop(self, count, per, body, first=0):
        start = self.n
        with self.eng.Fori(first, count) as i:
            self.shift = (i - first) * per if per else 0
            body(i)
            assert self.n - start == per, (self.n - start, per)
        self.n, self.shift = start + (count - first) * per, 0


def build(nc, x, c, positions, consts, decay, mask, vectors, ada, win, wout, wq, keys, u, v, out):
    ctx = ExitStack()
    with ctx:
        def sb(name, shape, dt=F32):
            return ctx.enter_context(nc.sbuf_tensor(name, shape, dt))

        def sem(name):
            return ctx.enter_context(nc.semaphore(name))

        big = sb("big", [P, NKEYS * SEQ])
        xT = sb("xT", [P, KC, SEQ])
        h_hi = sb("h_hi", [P, KC, SEQ], F32R)
        h_lo = sb("h_lo", [P, KC, SEQ], F32R)
        raw = sb("raw", [P, RING, D])
        w_hi = sb("w_hi", [P, 2, D], F32R)
        w_lo = sb("w_lo", [P, 2, D], F32R)
        p_hi = sb("p_hi", [P, 2, SEQ], F32R)
        p_lo = sb("p_lo", [P, 2, SEQ], F32R)
        cond = sb("cond", [P, D])
        onehot = sb("onehot", [P, 2, 2, BATCH, NKEYS])
        mod_ring1 = onehot[:].rearrange("p s a b n -> p s (a b n)")
        con = sb("con", [P, K_ALL])
        vec = sb("vec", [P, V_ALL])
        mod = sb("mod", [P, DEPTH, N_MOD])
        alpha = sb("alpha", [P, KC])
        rt = sb("rt", [P, 3, SEQ])
        mod_sum = sb("mod_sum", [P, MOD_SLOTS])
        small = sb("small", [P, 4, AH])
        ps = ctx.enter_context(nc.psum_tensor("ps", [P, 8, 512], F32))
        trig_dram = nc.dram_tensor("trig_scratch", [P, 4 * SEQ], F32, kind="Internal").ap()

        ident, ones, iota = (con[:, a:a + P] for a in (K_ID, K_ONE, K_IOTA))
        perm = [con[:, a:a + P] for a in (K_PR, K_PA)]
        eps = con[:, K_EPS:K_EPS + 1]

        def words(at, *shape):
            n = int(np.prod(shape))
            ap = big[:, at:at + n]
            if len(shape) == 1:
                return ap
            names = " ".join("abcd"[:len(shape)])
            return ap.rearrange(f"p ({names}) -> p {names}", **dict(zip("abcd", shape)))

        pj = words(W_PJ, N_WIN, SEQ)
        sq = words(W_SQ, KC, SEQ)
        hf = words(W_HF, KC, SEQ)
        decay_t = words(W_DECAY, RH, DW)
        trig = words(W_TRIG, 4, SEQ)
        mask_t = words(W_MASK, 2 * P)
        vtok = words(W_VTOK, TB, VW)
        s_att = words(W_S, AH, 2 * P)
        p_t = words(W_PT, AH, 2, P)
        ds_t = words(W_DS, RH, DW)
        gn_t = words(W_GN, 2, 2 * SEQ)
        ro = words(W_PJ, RH, SEQ)
        mod_ring0 = words(W_S, MOD_SLOTS, D)
        qt = words(W_QT, 2 * PH, SEQ)
        kt = words(W_KT, 2 * PH, NKEYS)
        score = words(W_SCORE, UNITS, 2 * NKEYS)
        res = words(W_RES, 3, UNITS, TOPK)
        acts = words(0, NKEYS, SEQ)
        rot_tmp = words(W_PT, 2, 2, SEQ)
        rs = words(W_VTOK, 3, SEQ)
        tw = words(W_HF, 8, SEQ)

        raw_in = [sem(f"raw_in{s}") for s in range(RING)]
        hi_ready, lo_ready, block_done, out_taken = map(sem, ("hi_ready", "lo_ready", "block_done", "out_taken"))
        small_in, x_in, c_in, pos_in = map(sem, ("small_in", "x_in", "c_in", "pos_in"))
        act_step, vec_step, unit_step = map(sem, ("act_step", "vec_step", "unit_step"))
        sig_c, angles, trig_made, trig_out, trig_in = map(sem, ("sig_c", "angles", "trig_made", "trig_out", "trig_in"))
        mod_in = [sem(f"mod_in{s}") for s in range(MOD_SLOTS)]
        mod_used = sem("mod_used")
        tables_in = sem("tables_in")
        keys_in = sem("keys_in")
        x_ready, sq_ready, ssq_ready, std_ready, hf_ready, hhi_ready, h_ready = map(sem, (
            "x_ready", "sq_ready", "ssq_ready", "std_ready", "hf_ready", "hhi_ready", "h_ready"))
        swapped, swap_used, rotated = map(sem, ("swapped", "swap_used", "rotated"))
        v_turned, v_copied = map(sem, ("v_turned", "v_copied"))
        ret_scored, ret_decayed, ret_out, ret_copied = map(sem, ("ret_scored", "ret_decayed", "ret_out", "ret_copied"))
        gn_mean, gn_centred, gn_sq, gn_var, gn_std, gn_rstd = map(sem, (
            "gn_mean", "gn_centred", "gn_sq", "gn_var", "gn_std", "gn_rstd"))
        gate_ab = sem("gate_ab")
        att_scored, att_max, att_exp, att_prob, att_turned, att_copied, att_out = map(sem, (
            "att_scored", "att_max", "att_exp", "att_prob", "att_turned", "att_copied", "att_out"))
        att_masked = sem("att_masked")
        merged, mhi_ready, mlo_ready = map(sem, ("merged", "mhi_ready", "mlo_ready"))
        score_ready, score_copied = map(sem, ("score_ready", "score_copied"))
        shifted, exped, gates_ready, choice_turned, choices_ready = map(sem, (
            "shifted", "exped", "gates_ready", "choice_turned", "choices_ready"))
        onehots, gated, gate_mat, gate_used = map(sem, ("onehots", "gated", "gate_mat", "gate_used"))
        phi_ready, plo_ready = map(sem, ("phi_ready", "plo_ready"))
        y_done, y_copied, y_turned, y_used = map(sem, ("y_done", "y_copied", "y_turned", "y_used"))
        result, stored = map(sem, ("result", "stored"))

        EV = B_V
        bank = lambda b: ps[:, b, :]
        E, M, Y = (0, 1), (2, 3), (4, 5, 6, 7)
        block = ctx.enter_context(nc.Block())

        @block.sync
        def _(sp):
            def load(src, i, j, base, l):
                n = base + RING * i + j
                ge(sp, lo_ready, n - RING + 1)
                sp.dma_start(raw[:, j, :], src(l, RING * i + j)).then_inc(raw_in[j], 16)

            srcs = [(N_WIN, lambda l, m: win[l, m]), (N_WOUT, lambda l, m: wout[l, m]),
                    (N_WQ, lambda l, m: wq[l, m]), (N_U, lambda l, m: u[l, m]), (N_V, lambda l, m: v[l, m])]
            for l in range(DEPTH):
                base = l * N_BLOCKS
                for count, src in srcs:
                    first = 0
                    if base == 0:
                        for j in range(RING):
                            load(src, 0, j, base, l)
                        first = 1
                    with sp.Fori(first, count // RING) as i:
                        for j in range(RING):
                            load(src, i, j, base, l)
                    base += count
            sp.wait_ge(result, 1)
            sp.dma_start(out, hf).then_inc(stored, 16)
            sp.wait_ge(stored, 16)

        @block.gpsimd
        def _(pool):
            pool.dma_start(con[:], consts).then_inc(small_in, 16)
            pool.dma_start(vec[:], vectors).then_inc(small_in, 16)
            pool.dma_start(cond[:], c.partition_broadcast(P)).then_inc(c_in, 16)
            pool.dma_start(rs[:, 0, :].bitcast(I32), positions.partition_broadcast(P)).then_inc(pos_in, 16)
            pool.dma_start(xT[:], x).then_inc(x_in, 16)

            def mod_load(l, g, s, used):
                ring, slots = ((mod_ring0, MOD_SLOTS), (mod_ring1, 2))[l]
                ge(pool, mod_used, used)
                pool.dma_start(ring[:, s, :], ada[l, slots * g + s]).then_inc(mod_in[s], 16)

            for s in range(MOD_SLOTS):
                mod_load(0, 0, s, 0)
            with pool.Fori(1, N_MOD // MOD_SLOTS) as g:
                for s in range(MOD_SLOTS):
                    mod_load(0, g, s, g * MOD_SLOTS - MOD_SLOTS + s + 1)
            pool.wait_ge(trig_made, 1)
            pool.dma_start(trig_dram, words(W_TRIG, 4 * SEQ)).then_inc(trig_out, 16)
            pool.wait_ge(trig_out, 16)
            for l in range(DEPTH):
                if l:
                    pool.wait_ge(y_done, l)
                    pool.dma_start(words(W_TRIG, 4 * SEQ), trig_dram).then_inc(trig_in, 16)
                pool.dma_start(words(W_DECAY, RH * DW), decay).then_inc(tables_in, 16)
                pool.dma_start(mask_t, mask).then_inc(tables_in, 16)
                pool.wait_ge(out_taken, l * EV + C_GB)
                for k in range(KC // 2):
                    a = C_RG + 2 * k
                    b = C_GA + 2 * k
                    nc.gpsimd.tensor_tensor(pj[:, a:a + 2, :], pj[:, a:a + 2, :], pj[:, b:b + 2, :],
                                            ALU.mult).then_inc(gate_ab, 1)
                pool.wait_ge(ret_decayed, (l + 1) * RH)
                pool.dma_start(words(W_KT, 2 * PH * NKEYS), keys[l]).then_inc(keys_in, 16)
                if l + 1 < DEPTH:
                    pool.wait_ge(gate_used, (l + 1) * N_GATE)
                    for s in range(2):
                        mod_load(1, 0, s, 0)
                    with pool.Fori(1, N_MOD // 2) as g:
                        for s in range(2):
                            mod_load(1, g, s, N_MOD + g * 2 - 2 + s + 1)

        @block.scalar
        def _(act):
            st = Steps(act, act_step)

            def round_hi(n, j):
                act.wait_ge(raw_in[j], (n - j) * (16 // RING) + 16)
                ge(act, block_done, n - 1)
                nc.scalar.copy(w_hi[:, j % 2, :], raw[:, j, :]).then_inc(hi_ready, 1)

            def take(n, dst, func, j):
                act.wait_ge(block_done, n + 1)
                nc.scalar.activation(dst, bank(E[j % 2])[:, 0:SEQ], func).then_inc(out_taken, 1)

            def stage(l, base, count, dst, func):
                n0 = l * N_BLOCKS + base

                def body(i):
                    for j in range(RING):
                        n = n0 + RING * i + j
                        if dst is not None:
                            take(n, dst(RING * i + j), func, j)
                        round_hi(n + 2, (j + 2) % RING)
                st.loop(count // RING, 0, body)

            act.wait_ge(c_in, 16)
            nc.scalar.activation(words(W_PJ, D), cond[:], ACT.Sigmoid).then_inc(sig_c, 1)
            act.wait_ge(angles, 4)
            nc.scalar.activation(words(W_TRIG, 4 * SEQ), words(W_HF, 4 * SEQ), ACT.Sin).then_inc(trig_made, 1)
            round_hi(0, 0)
            round_hi(1, 1)

            def norm(q, src_ready, src_count, final=False):
                act.wait_ge(src_ready, src_count)
                if q == 0:
                    act.wait_ge(trig_made, 1)
                for k in range(2):
                    nc.scalar.activation(sq[:, 4 * k:4 * k + 4, :], xT[:, 4 * k:4 * k + 4, :],
                                         ACT.Square).then_inc(sq_ready, 1)
                act.wait_ge(ssq_ready, q + 1)
                nc.scalar.activation(rs[:, 1, :], bank(M[0])[:, 0:SEQ], ACT.Sqrt, bias=eps,
                                     scale=1.0 / D).then_inc(std_ready, 1)
                if final:
                    return
                for k in range(2):
                    act.wait_ge(hf_ready, 2 * q + k + 1)
                    nc.scalar.copy(h_hi[:, 4 * k:4 * k + 4, :], hf[:, 4 * k:4 * k + 4, :]).then_inc(hhi_ready, 1)

            for l in range(DEPTH):
                if l == 0:
                    act.wait_ge(small_in, 32)
                norm(2 * l, x_in if l == 0 else x_ready, 16 if l == 0 else 2 * l)
                stage(l, B_WIN, C_RG, lambda m: pj[:, ds(m, 1), :] if not isinstance(m, int) else pj[:, m:m + 1, :],
                      ACT.Copy)
                stage(l, B_WIN + C_RG, C_GA - C_RG, lambda m: pj[:, ds(m + C_RG, 1), :], ACT.Silu)
                stage(l, B_WIN + C_GA, N_WIN - C_GA, lambda m: pj[:, ds(m + C_GA, 1), :], ACT.Sigmoid)
                for g in range(5):
                    act.wait_ge(v_turned, 5 * l + g + 1)
                    o = vtok[:, :, 2 * P * g:2 * P * (g + 1)].rearrange("p t (c n) -> p c t n", c=2)
                    nc.scalar.copy(o, bank(M[g % 2]).rearrange("p (c t n) -> p c t n", c=2, t=TB)).then_inc(v_copied, 1)
                for g in range(4):
                    act.wait_ge(ret_out, 4 * l + g + 1)
                    nc.scalar.copy(ro[:, 2 * g:2 * g + 2, :], bank(Y[g]).rearrange("p (a t) -> p a t", a=2)
                                   ).then_inc(ret_copied, 1)
                for g in range(4):
                    act.wait_ge(gn_centred, 4 * l + g + 1)
                    if g >= 2:
                        act.wait_ge(gn_rstd, 4 * l + g - 1)
                    nc.scalar.activation(gn_t[:, g % 2, :], ro[:, 2 * g:2 * g + 2, :], ACT.Square).then_inc(gn_sq, 1)
                    act.wait_ge(gn_var, 4 * l + g + 1)
                    nc.scalar.activation(gn_t[:, g % 2, :], bank(Y[g]), ACT.Sqrt, bias=eps,
                                         scale=1.0 / RDV).then_inc(gn_std, 1)
                for b in range(TB):
                    w = P * (b + 1)
                    q = TB * l + b
                    act.wait_ge(att_max, q + 1)
                    nc.scalar.activation(small[:, 3, :], small[:, 3, :], ACT.Exp)
                    for h in range(AH):
                        last = nc.scalar.activation(s_att[:, h, 0:w], s_att[:, h, 0:w], ACT.Exp,
                                                    bias=small[:, 1, h:h + 1], accum_out=small[:, 2, h:h + 1])
                        if h % 4 == 3:
                            last.then_inc(att_exp, 1)
                    for g in range(4 * (b + 1)):
                        act.wait_ge(att_turned, 12 * l + 4 * b + g + 1)
                        if b == 0:
                            o = p_t[:, 4 * g:4 * g + 4, 0, :]
                            i_ = bank(M[g % 2]).rearrange("p (h n) -> p h n", h=4)
                        else:
                            o = p_t[:, 2 * g:2 * g + 2, :, :]
                            i_ = bank(M[g % 2]).rearrange("p (h k n) -> p h k n", h=2, k=2)
                        nc.scalar.copy(o, i_).then_inc(att_copied, 1)
                for k in range(2):
                    act.wait_ge(merged, 2 * l + k + 1)
                    nc.scalar.copy(h_hi[:, 4 * k:4 * k + 4, :], hf[:, 4 * k:4 * k + 4, :]).then_inc(mhi_ready, 1)
                stage(l, B_WOUT, N_WOUT, None, None)
                norm(2 * l + 1, x_ready, 2 * l + 1)
                stage(l, B_WQ, N_WQ, lambda m: qt[:, ds(m, 1), :], ACT.Copy)
                for g in range(8):
                    act.wait_ge(score_ready, 8 * l + g + 1)
                    nc.scalar.copy(score[:, 2 * g:2 * g + 2, :],
                                   bank(M[g % 2]).rearrange("p (a n) -> p a n", a=2)).then_inc(score_copied, 1)
                stage(l, B_U, N_U1, lambda m: acts[:, ds(m, 1), :], ACT.Gelu)
                act.wait_ge(shifted, l + 1)
                nc.scalar.activation(res[:, 2, :, :], res[:, 2, :, :], ACT.Exp).then_inc(exped, 1)
                act.wait_ge(choices_ready, l + 1)
                stage(l, B_U + N_U1, N_U - N_U1, lambda m: acts[:, ds(m + N_U1, 1), :], ACT.Gelu)

                def gate(i):
                    for s in range(2):
                        act.wait_ge(onehots, l * N_GATE + 2 * i + s + 1)
                        for t in range(BATCH):
                            last = nc.scalar.activation(onehot[:, s, 1, t, :], onehot[:, s, 1, t, :], ACT.Copy,
                                                        scale=rt[:, 2, ds(i * 2 * BATCH + s * BATCH + t, 1)])
                        last.then_inc(gated, 1)
                st.loop(N_GATE // 2, 0, gate)

                def round_p(m, s):
                    nc.scalar.copy(p_hi[:, s, :], acts[:, ds(m, 1), :].rearrange("p a t -> p (a t)")
                                   ).then_inc(phi_ready, 1)

                def outputs(i, end=False):
                    for j in range(RING):
                        m = RING * i + j
                        n = l * N_BLOCKS + B_V + m
                        if not (end and j >= 2):
                            act.wait_ge(block_done, n + 1)
                            round_p(m + 2, j % 2)
                        if not (end and j >= 2 and l == DEPTH - 1):
                            round_hi(n + 2, (j + 2) % RING)
                act.wait_ge(gate_used, (l + 1) * N_GATE)
                for m in range(2):
                    round_p(m, m)
                st.loop(N_V // RING - 1, 0, outputs)
                outputs(N_V // RING - 1, end=True)
                for g in range(4):
                    act.wait_ge(y_done, l + 1)
                    nc.scalar.copy(words(W_PJ, 4, 512)[:, g, :], bank(Y[g])).then_inc(y_copied, 1)
            norm(2 * DEPTH, x_ready, 2 * DEPTH, final=True)

        @block.vector
        def _(dve):
            st = Steps(dve, vec_step)
            us = Steps(dve, unit_step)
            tt, ts, stt = nc.vector.tensor_tensor, nc.vector.tensor_scalar, nc.vector.scalar_tensor_tensor

            def low(n, j):
                dve.wait_ge(hi_ready, n + 1)
                tt(w_lo[:, j % 2, :], raw[:, j, :], w_hi[:, j % 2, :].bitcast(F32), ALU.subtract).then_inc(lo_ready, 1)

            def mod_block(l, s, uses):
                ring = (mod_ring0, mod_ring1)[l]
                dve.wait_ge(mod_in[s], uses)
                nc.vector.tensor_tensor_reduce(ring[:, s, :], ring[:, s, :], cond[:], 1.0, 0.0, ALU.mult, ALU.add,
                                               mod_sum[:, s:s + 1]).then_inc(mod_used, 1)

            def mod_bias(l, n, count, used):
                dve.wait_ge(mod_used, used)
                st.link(tt(mod[:, l, ds(n, count)], mod_sum[:, 0:count], vec[:, ds(V_ADAB + l * N_MOD + n, count)],
                           ALU.add))

            dve.wait_ge(small_in, 32)
            dve.wait_ge(sig_c, 1)
            st.link(tt(cond[:], cond[:], words(W_PJ, D), ALU.mult))
            dve.wait_ge(pos_in, 16)
            st.link(nc.vector.tensor_copy(rs[:, 1, :], rs[:, 0, :].bitcast(I32)))
            for a in range(2):
                cosw, sinw, ang, turns = tw[:, 2 * a, :], tw[:, 2 * a + 1, :], tw[:, 4, :], tw[:, 5, :]
                st.link(ts(ang, rs[:, 1, :], con[:, K_FR + a:K_FR + a + 1], None, ALU.mult))
                st.link(ts(turns, ang, float(1 / (2 * np.pi)), MAGIC, ALU.mult, ALU.add))
                st.link(ts(turns, turns, MAGIC, None, ALU.subtract))
                for part in (TWO_PI_1, TWO_PI_2, TWO_PI_3):
                    st.link(stt(ang, turns, -part, ang, ALU.mult, ALU.add))
                ts(sinw, ang, PI_SAFE, -PI_SAFE, ALU.min, ALU.max).then_inc(angles, 1)
                st.link(ts(ang, ang, float(np.pi / 2), None, ALU.add))
                st.link(ts(turns, ang, PI_SAFE, -2 * float(np.pi), ALU.is_gt, ALU.mult))
                st.link(tt(ang, ang, turns, ALU.add))
                ts(cosw, ang, PI_SAFE, -PI_SAFE, ALU.min, ALU.max).then_inc(angles, 1)
                dve.wait_ge(angles, 2 * a + 2)
            low(0, 0)
            for g in range(MOD_FIRST // MOD_SLOTS):
                for s in range(MOD_SLOTS):
                    mod_block(0, s, 16 * (g + 1))
                mod_bias(0, g * MOD_SLOTS, MOD_SLOTS, (g + 1) * MOD_SLOTS)

            def norm(q, gain, sc, sh, final=False):
                l = q // 2
                if not final:
                    st.link(stt(alpha[:], mod[:, l, sc:sc + KC], 1.0, vec[:, gain:gain + KC], ALU.add, ALU.mult))
                dve.wait_ge(std_ready, q + 1)
                st.link(ts(rs[:, 0, :], bank(M[0])[:, 0:SEQ], 1.0 / D, EPS, ALU.mult, ALU.add))
                st.link(nc.vector.reciprocal(rs[:, 1, :], rs[:, 1, :]))
                st.link(tt(rs[:, 2, :], rs[:, 1, :], rs[:, 1, :], ALU.mult))
                st.link(tt(rs[:, 2, :], rs[:, 2, :], rs[:, 0, :], ALU.mult))
                st.link(ts(rs[:, 2, :], rs[:, 2, :], -0.5, 1.5, ALU.mult, ALU.add))
                st.link(tt(rs[:, 1, :], rs[:, 1, :], rs[:, 2, :], ALU.mult))
                for k in range(2):
                    r = rs[:, 1:2, :].broadcast_to([P, 4, SEQ])
                    st.done(tt(hf[:, 4 * k:4 * k + 4, :], xT[:, 4 * k:4 * k + 4, :], r, ALU.mult))
                st.wait()
                for k in range(KC):
                    if final:
                        last = ts(hf[:, k, :], hf[:, k, :], vec[:, gain + k:gain + k + 1], None, ALU.mult)
                    else:
                        last = ts(hf[:, k, :], hf[:, k, :], alpha[:, k:k + 1], mod[:, l, sh + k:sh + k + 1],
                                  ALU.mult, ALU.add)
                    if not final and k % 4 == 3:
                        last.then_inc(hf_ready, 1)
                if final:
                    last.then_inc(result, 1)
                    return
                dve.wait_ge(hhi_ready, 2 * q + 2)
                tt(h_lo[:], hf[:], h_hi[:].bitcast(F32), ALU.subtract).then_inc(h_ready, 1)

            def stage(l, base, count, extra=None, per=0, last_one=True):
                n0 = l * N_BLOCKS + base

                def body(i):
                    for j in range(RING):
                        low(n0 + RING * i + j + 1, (j + 1) % RING)
                        if extra is not None:
                            extra(i, j)
                st.loop(count // RING, per, body)

            for l in range(DEPTH):
                norm(2 * l, V_N1 + KC * l, SC1, SH1)
                if l == 0:
                    def rest(i):
                        for s in range(MOD_SLOTS):
                            low(MOD_SLOTS * i + s + 1, (s + 1) % RING)
                            mod_block(0, s, i * 16 + 16 * (MOD_FIRST // MOD_SLOTS + 1))
                        mod_bias(0, i * MOD_SLOTS + MOD_FIRST, MOD_SLOTS, (i + 1) * MOD_SLOTS + MOD_FIRST)
                    st.loop((N_MOD - MOD_FIRST) // MOD_SLOTS, 1, rest)
                    stage(l, B_WIN + N_MOD - MOD_FIRST, N_WIN - N_MOD + MOD_FIRST)
                else:
                    stage(l, B_WIN, N_WIN)
                if l:
                    dve.wait_ge(trig_in, 16 * l)
                else:
                    dve.wait_ge(trig_made, 1)
                for g in range(N_ROT):
                    a = 0 if g < 4 else 2
                    cosb = trig[:, a:a + 1, :].broadcast_to([P, 2, SEQ])
                    sinb = trig[:, a + 1:a + 2, :].broadcast_to([P, 2, SEQ])
                    x2 = pj[:, 2 * g:2 * g + 2, :]
                    dve.wait_ge(swapped, N_ROT * l + g + 1)
                    st.done(tt(x2, x2, cosb, ALU.mult))
                    if g >= 2:
                        dve.wait_ge(rotated, N_ROT * l + g - 1)
                    tt(rot_tmp[:, g % 2], bank(M[g % 2]).rearrange("p (a t) -> p a t", a=2), sinb,
                       ALU.mult).then_inc(swap_used, 1)
                    dve.wait_ge(swap_used, N_ROT * l + g + 1)
                    st.wait()
                    tt(x2, x2, rot_tmp[:, g % 2], ALU.add).then_inc(rotated, 1)
                dve.wait_ge(tables_in, 32 * (l + 1))
                for h in range(RH):
                    dve.wait_ge(ret_scored, RH * l + h + 1)
                    tt(ds_t[:, h, :], bank(E[h % 2])[:, 0:DW], decay_t[:, h, :], ALU.mult).then_inc(ret_decayed, 1)
                dve.wait_ge(gate_ab, 4 * (l + 1))
                for g in range(4):
                    r2 = ro[:, 2 * g:2 * g + 2, :]
                    m2 = bank(M[g % 2]).rearrange("p (a t) -> p a t", a=2)
                    dve.wait_ge(gn_mean, 4 * l + g + 1)
                    stt(r2, m2, -1.0 / RDV, r2, ALU.mult, ALU.add).then_inc(gn_centred, 1)
                for g in range(4):
                    r2 = ro[:, 2 * g:2 * g + 2, :]
                    t2 = gn_t[:, g % 2, :].rearrange("p (a t) -> p a t", a=2)
                    dve.wait_ge(gn_std, 4 * l + g + 1)
                    st.link(nc.vector.reciprocal(gn_t[:, g % 2, :], gn_t[:, g % 2, :]))
                    for a in range(2):
                        col = V_GN + KC * l + 2 * g + a
                        last = stt(r2[:, a, :], r2[:, a, :], vec[:, col:col + 1], t2[:, a, :], ALU.mult, ALU.mult)
                    last.then_inc(gn_rstd, 1)
                    dve.wait_ge(gn_rstd, 4 * l + g + 1)
                    st.done(tt(r2, r2, pj[:, C_RG + 2 * g:C_RG + 2 * g + 2, :], ALU.mult))
                sink = vec[:, V_SINK + AH * l:V_SINK + AH * (l + 1)]
                for b in range(TB):
                    w = P * (b + 1)
                    q = TB * l + b
                    if b:
                        dve.wait_ge(att_turned, 12 * l + 4)
                    for h in range(AH):
                        if h % 2 == 0:
                            dve.wait_ge(att_scored, 8 * q + h // 2 + 1)
                        last = nc.vector.tensor_tensor_reduce(
                            s_att[:, h, 0:w], bank(E[h // 2 % 2])[:, 2 * P * (h % 2):2 * P * (h % 2) + w],
                            mask_t[:, 2 * P - w:2 * P], ATT_SCALE, sink[:, h:h + 1], ALU.add, ALU.max,
                            small[:, 0, h:h + 1])
                        if h % 2:
                            last.then_inc(att_masked, 1)
                    dve.wait_ge(att_masked, 8 * (q + 1))
                    st.done(ts(small[:, 1, :], small[:, 0, :], -1.0, None, ALU.mult))
                    tt(small[:, 3, :], sink, small[:, 0, :], ALU.subtract).then_inc(att_max, 1)
                    for g in range(4):
                        hs = slice(4 * g, 4 * g + 4)
                        dve.wait_ge(att_exp, 4 * q + g + 1)
                        st.link(tt(small[:, 2, hs], small[:, 2, hs], small[:, 3, hs], ALU.add))
                        st.link(nc.vector.reciprocal(small[:, 2, hs], small[:, 2, hs]))
                        for h in range(4 * g, 4 * g + 4):
                            last = ts(s_att[:, h, 0:w], s_att[:, h, 0:w], small[:, 2, h:h + 1], None, ALU.mult)
                        last.then_inc(att_prob, 1)
                dve.wait_ge(out_taken, l * EV + N_WIN)
                dve.wait_ge(att_out, TB * (l + 1))
                for g in range(4):
                    st.done(tt(hf[:, 2 * g:2 * g + 2, :], bank(Y[g]).rearrange("p (a t) -> p a t", a=2),
                               pj[:, C_GB + 2 * g:C_GB + 2 * g + 2, :], ALU.mult))
                st.wait()
                for k in range(2):
                    tt(hf[:, 4 * k:4 * k + 4, :], hf[:, 4 * k:4 * k + 4, :], ro[:, 4 * k:4 * k + 4, :],
                       ALU.add).then_inc(merged, 1)
                dve.wait_ge(mhi_ready, 2 * (l + 1))
                tt(h_lo[:], hf[:], h_hi[:].bitcast(F32), ALU.subtract).then_inc(mlo_ready, 1)

                def add_mixer(i, j):
                    n = l * N_BLOCKS + B_WOUT + RING * i + j
                    dve.wait_ge(block_done, n + 1)
                    xk = xT[:, ds(RING * i + j, 1), :]
                    stt(xk, bank(E[j % 2])[:, 0:SEQ].rearrange("p (a t) -> p a t", a=1),
                        mod[:, l, ds(G1 + RING * i + j, 1)], xk, ALU.mult, ALU.add).then_inc(out_taken, 1)
                stage(l, B_WOUT, N_WOUT, add_mixer)
                dve.wait_ge(out_taken, l * EV + B_WQ)
                nc.vector.tensor_copy(small[:, 0, 0:1], small[:, 0, 0:1]).then_inc(x_ready, 1)
                norm(2 * l + 1, V_N2 + KC * l, SC2, SH2)
                stage(l, B_WQ, N_WQ)
                dve.wait_ge(score_copied, 8 * (l + 1))
                w0 = W_STAGE
                s0, s1, cand, cand1 = (words(w0 + 2 * P * a, 2 * P) for a in range(4))
                pick = words(w0 + 1024, 2, TOPK, TOPK)
                val, idf = words(w0 + 1536, 2, TOPK), words(w0 + 1568, 2, TOPK)
                idx = words(w0 + 1600, 2, TOPK).bitcast(U32)
                top, pos = words(w0 + 1632, TOPK), words(w0 + 1648, TOPK).bitcast(U32)
                split = words(w0 + 1664, 2, TOPK).bitcast(U32)
                splf = words(w0 + 1696, 2, TOPK)
                mx, mi, mr = nc.vector.max, nc.vector.max_index, nc.vector.match_replace

                def top16(val_, idx_, src, work):
                    us.wait()
                    us.done(mx(val_[:, 0:8], src))
                    us.wait()
                    a = us.done(mr(work, val_[:, 0:8], src, REMOVED))
                    us.done(mi(idx_[:, 0:8], val_[:, 0:8], src))
                    us.wait(a)
                    us.done(mx(val_[:, 8:16], work))
                    us.wait()
                    us.done(mi(idx_[:, 8:16], val_[:, 8:16], work))

                def unit(i, j):
                    if j == 0:
                        us.done(nc.vector.tensor_copy(s0, score[:, ds(i, 1), :].rearrange("p a n -> p (a n)")))
                        top16(val[:, 0, :], idx[:, 0, :], s0[:, 0:P], s1[:, 0:P])
                    if j == 1:
                        top16(val[:, 1, :], idx[:, 1, :], s0[:, P:2 * P], s1[:, P:2 * P])
                        us.wait()
                        us.done(nc.vector.tensor_copy(idf, idx))
                        us.done(tt(cand.rearrange("p (a b) -> p a b", a=TOPK),
                                   val[:, 0, :].unsqueeze(2).broadcast_to([P, TOPK, TOPK]),
                                   val[:, 1, :].unsqueeze(1).broadcast_to([P, TOPK, TOPK]), ALU.add))
                    if j == 2:
                        top16(top, pos, cand, cand1)
                        us.wait()
                        us.done(ts(split[:, 0, :], pos, 4, None, ALU.logical_shift_right))
                        us.done(ts(split[:, 1, :], pos, TOPK - 1, None, ALU.bitwise_and))
                        us.done(nc.vector.tensor_copy(res[:, 2, ds(i, 1), :].rearrange("p a k -> p (a k)"), top))
                        us.wait()
                    if j == 3:
                        us.link(nc.vector.tensor_copy(splf, split))
                        for a in range(2):
                            us.done(tt(pick[:, a], splf[:, a, :].unsqueeze(2).broadcast_to([P, TOPK, TOPK]),
                                       iota[:, 0:TOPK].unsqueeze(1).broadcast_to([P, TOPK, TOPK]), ALU.is_equal))
                        us.wait()
                        for a in range(2):
                            us.done(tt(pick[:, a], pick[:, a],
                                       idf[:, a, :].unsqueeze(1).broadcast_to([P, TOPK, TOPK]), ALU.mult))
                        us.wait()
                        for a in range(2):
                            us.done(nc.vector.tensor_reduce(res[:, a, ds(i, 1), :].rearrange("p a k -> p (a k)"),
                                                            pick[:, a], AX_X, ALU.add))
                        us.wait()
                        dve.sem_clear(unit_step)
                        us.n = 0

                n0 = l * N_BLOCKS + B_U

                def units(i):
                    for c in range(2):
                        for j in range(UNIT_BLOCKS):
                            m = UNIT_BLOCKS * c + j
                            low(n0 + 2 * UNIT_BLOCKS * i + m + 1, (m + 1) % RING)
                            if j < 4:
                                unit(2 * i + c, j)
                st.loop(UNITS // 2, 0, units)
                gt = res[:, 2, :, :]
                st.link(tt(s0.rearrange("p (a b) -> p a b", a=UNITS), gt,
                           gt[:, :, 0:1].broadcast_to([P, UNITS, TOPK]), ALU.subtract))
                nc.vector.tensor_copy(gt, s0.rearrange("p (a b) -> p a b", a=UNITS)).then_inc(shifted, 1)
                dve.wait_ge(exped, l + 1)
                st.link(nc.vector.tensor_reduce(top, gt, AX_X, ALU.add))
                st.link(nc.vector.reciprocal(top, top))
                tt(gt, gt, top.unsqueeze(2).broadcast_to([P, UNITS, TOPK]), ALU.mult).then_inc(gates_ready, 1)
                dve.wait_ge(choice_turned, l + 1)
                st.done(nc.vector.tensor_copy(rt[:, 0:2, :], bank(M[0]).rearrange("p (a t) -> p a t", a=2)))
                nc.vector.tensor_copy(rt[:, 2, :], bank(M[1])[:, 0:SEQ]).then_inc(choices_ready, 1)
                stage(l, B_U + N_U1, N_U - N_U1)
                st.wait()
                dve.wait_ge(choices_ready, l + 1)
                dve.wait_ge(out_taken, (l + 1) * EV)

                def hot(b, s):
                    for a in range(2):
                        last = tt(onehot[:, s, a], rt[:, a, ds(b * BATCH, BATCH)].unsqueeze(2).broadcast_to([P, BATCH, P]),
                                  iota.unsqueeze(1).broadcast_to([P, BATCH, P]), ALU.is_equal)
                    last.then_inc(onehots, 1)

                def weigh(b, s):
                    dve.wait_ge(gate_mat, l * N_GATE + b + 1)
                    a4 = acts[:, :, ds(b * BATCH, BATCH)]
                    tt(a4, a4, bank(M[s]).rearrange("p (i t) -> p i t", t=BATCH), ALU.mult).then_inc(gate_used, 1)

                def gates(i):
                    for s in range(2):
                        hot(2 * i + s + 1, (s + 1) % 2)
                        weigh(2 * i + s, s)
                hot(0, 0)
                st.loop(N_GATE // 2 - 1, 0, gates)
                hot(N_GATE - 1, 1)
                weigh(N_GATE - 2, 0)
                weigh(N_GATE - 1, 1)
                n0 = l * N_BLOCKS + B_V
                dve.wait_ge(gate_used, (l + 1) * N_GATE)

                def low_p(m, s):
                    dve.wait_ge(phi_ready, l * N_V + m + 1)
                    tt(p_lo[:, s, :], acts[:, ds(m, 1), :].rearrange("p a t -> p (a t)"),
                       p_hi[:, s, :].bitcast(F32), ALU.subtract).then_inc(plo_ready, 1)

                def outputs(i, ada_on=False, end=False):
                    for j in range(RING):
                        if not (end and j == RING - 1):
                            low_p(RING * i + j + 1, (j + 1) % 2)
                        if not (end and j == RING - 1 and l == DEPTH - 1):
                            low(n0 + RING * i + j + 1, (j + 1) % RING)
                        if ada_on and j % 2:
                            mod_block(1, j // 2, i * 16 + 16 * (N_MOD // MOD_SLOTS + 1))
                    if ada_on:
                        mod_bias(1, 2 * i, 2, 2 * i + N_MOD + 2)
                low_p(0, 0)
                first = 0
                if l + 1 < DEPTH:
                    st.loop(N_MOD // 2, 1, lambda i: outputs(i, True))
                    first = N_MOD // 2
                st.loop(N_V // RING - 1, 0, outputs, first=first)
                outputs(N_V // RING - 1, end=True)
                for k in range(KC):
                    dve.wait_ge(y_turned, KC * l + k + 1)
                    stt(xT[:, k, :], bank(M[k % 2])[:, 0:SEQ], mod[:, l, G2 + k:G2 + k + 1], xT[:, k, :],
                        ALU.mult, ALU.add).then_inc(y_used, 1)
                dve.wait_ge(y_used, KC * (l + 1))
                nc.vector.tensor_copy(small[:, 0, 0:1], small[:, 0, 0:1]).then_inc(x_ready, 1)
            norm(2 * DEPTH, V_FIN, None, None, final=True)

        @block.tensor
        def _(pe):
            mm, turn = nc.tensor.matmul, nc.tensor.transpose

            def project(n, e, j):
                s = j % 2
                pe.wait_ge(hi_ready, n + 1)
                ge(pe, out_taken, e - 1)
                o = bank(E[s])[:, 0:SEQ]
                for k in range(KC):
                    w = w_hi[:, s, P * k:P * (k + 1)]
                    mm(o, w, h_hi[:, k, :], start=(k == 0), stop=False)
                    mm(o, w, h_lo[:, k, :], start=False, stop=False)
                pe.wait_ge(lo_ready, n + 1)
                for k in range(KC):
                    last = mm(o, w_lo[:, s, P * k:P * (k + 1)], h_hi[:, k, :], start=False, stop=(k == KC - 1))
                last.then_inc(block_done, 1)

            def stage(l, base, count):
                def body(i):
                    for j in range(RING):
                        project(l * N_BLOCKS + base + RING * i + j, l * EV + base + RING * i + j, j)
                first = 0
                if l == 0 and base == 0:
                    body(0)
                    first = 1
                with pe.Fori(first, count // RING) as i:
                    body(i)

            def norm(q):
                for k in range(KC):
                    if k % 4 == 0:
                        pe.wait_ge(sq_ready, 2 * q + k // 4 + 1)
                    last = mm(bank(M[0])[:, 0:SEQ], ones, sq[:, k, :], start=(k == 0), stop=(k == KC - 1))
                last.then_inc(ssq_ready, 1)

            pe.wait_ge(small_in, 32)
            for l in range(DEPTH):
                norm(2 * l)
                pe.wait_ge(h_ready, 2 * l + 1)
                stage(l, B_WIN, N_WIN)
                pe.wait_ge(out_taken, l * EV + N_WIN)
                for g in range(N_ROT):
                    if g >= 2:
                        pe.wait_ge(swap_used, N_ROT * l + g - 1)
                    for a in range(2):
                        last = mm(bank(M[g % 2])[:, SEQ * a:SEQ * (a + 1)], perm[0 if g < 4 else 1],
                                  pj[:, 2 * g + a, :], start=True, stop=True)
                    last.then_inc(swapped, 1)
                for g in range(5):
                    if g < 2:
                        pe.wait_ge(swap_used, N_ROT * (l + 1))
                    else:
                        pe.wait_ge(v_copied, 5 * l + g - 1)
                    for a in range(2):
                        for t in range(TB):
                            last = turn(bank(M[g % 2])[:, (TB * a + t) * P:(TB * a + t + 1) * P],
                                        pj[:, C_RV + 2 * g + a, P * t:P * (t + 1)], ident)
                    last.then_inc(v_turned, 1)
                pe.wait_ge(rotated, N_ROT * (l + 1))
                for h in range(RH):
                    if h >= 2:
                        pe.wait_ge(ret_decayed, RH * l + h - 1)
                    r = slice(RDK * (h % 2), RDK * (h % 2 + 1))
                    q_, k_ = pj[r, C_RQ + h // 2, :], pj[r, C_RK + h // 2, :]
                    mm(bank(E[h % 2])[:, 0:SEQ], k_[:, 0:P], q_, start=True, stop=True)
                    mm(bank(E[h % 2])[:, SEQ:DW], k_[:, P:SEQ], q_[:, P:SEQ], start=True, stop=True
                       ).then_inc(ret_scored, 1)
                pe.wait_ge(v_copied, 5 * (l + 1))
                for h in range(RH):
                    pe.wait_ge(ret_decayed, RH * l + h + 1)
                    o = bank(Y[h // 2])[:, SEQ * (h % 2):SEQ * (h % 2 + 1)]
                    mm(o, vtok[:, 0, RDV * h:RDV * (h + 1)], ds_t[:, h, 0:SEQ], start=True, stop=False)
                    last = mm(o[:, P:SEQ], vtok[:, 1, RDV * h:RDV * (h + 1)], ds_t[:, h, SEQ:DW], start=False, stop=True)
                    if h % 2:
                        last.then_inc(ret_out, 1)
                for g in range(4):
                    pe.wait_ge(ret_copied, 4 * l + g + 1)
                    if g >= 2:
                        pe.wait_ge(gn_centred, 4 * l + g - 1)
                    mm(bank(M[g % 2]), ones, ro[:, 2 * g:2 * g + 2, :], start=True, stop=True).then_inc(gn_mean, 1)
                for g in range(4):
                    pe.wait_ge(gn_sq, 4 * l + g + 1)
                    mm(bank(Y[g]), ones, gn_t[:, g % 2, :], start=True, stop=True).then_inc(gn_var, 1)
                for b in range(TB):
                    w = P * (b + 1)
                    q = TB * l + b
                    for h in range(AH):
                        kv = h // (AH // AKV)
                        r = slice(AHD * (kv % 2), AHD * (kv % 2 + 1))
                        if h % 2 == 0 and h >= 4 or h % 2 == 0 and b:
                            pe.wait_ge(att_masked, 8 * q + h // 2 - 1)
                        aq = pj[r, C_AQ + 4 * (kv // 2) + h % 4, P * b:P * (b + 1)]
                        ak = pj[r, C_AK + kv // 2, SEQ - 2 * P:w]
                        last = mm(bank(E[h // 2 % 2])[:, 2 * P * (h % 2):2 * P * (h % 2) + w], aq, ak, start=True, stop=True)
                        if h % 2:
                            last.then_inc(att_scored, 1)
                    if b == 0:
                        pe.wait_ge(gn_centred, 4 * (l + 1))
                    for g in range(4 * (b + 1)):
                        hs = 4 // (b + 1)
                        pe.wait_ge(att_prob, 4 * q + (g * hs + hs - 1) // 4 + 1)
                        if b or g >= 2:
                            pe.wait_ge(att_copied, 12 * l + 4 * b + g - 1)
                        for a in range(4):
                            h, kb = (4 * g + a, 0) if b == 0 else (2 * g + a // 2, a % 2)
                            last = turn(bank(M[g % 2])[:, P * a:P * (a + 1)], s_att[:, h, P * kb:P * (kb + 1)], ident)
                        last.then_inc(att_turned, 1)
                    if b == 0:
                        pe.wait_ge(gn_std, 4 * (l + 1))
                    pe.wait_ge(att_copied, 12 * l + 4 * b + 4 * (b + 1))
                    for h in range(AH):
                        kv = h // (AH // AKV)
                        col = SEQ * (h // 2 % 2) + P * b
                        o = ps[AHD * (h % 2):AHD * (h % 2 + 1), Y[h // 4], col:col + P]
                        for kb in range(b + 1):
                            last = mm(o, vtok[:, kb, D + AHD * kv:D + AHD * (kv + 1)], p_t[:, h, kb, :],
                                      start=(kb == 0), stop=(kb == b))
                    last.then_inc(att_out, 1)
                pe.wait_ge(mlo_ready, l + 1)
                stage(l, B_WOUT, N_WOUT)
                norm(2 * l + 1)
                pe.wait_ge(h_ready, 2 * l + 2)
                stage(l, B_WQ, N_WQ)
                pe.wait_ge(keys_in, 16 * (l + 1))
                pe.wait_ge(out_taken, l * EV + B_U)
                for g in range(8):
                    if g >= 2:
                        pe.wait_ge(score_copied, 8 * l + g - 1)
                    for a in range(4):
                        unit, side = 2 * g + a // 2, a % 2
                        t, h = unit // PH, unit % PH
                        last = mm(bank(M[g % 2])[:, P * a:P * (a + 1)], qt[:, 2 * h + side, P * t:P * (t + 1)],
                                  kt[:, 2 * h + side, :], start=True, stop=True)
                    last.then_inc(score_ready, 1)
                stage(l, B_U, N_U1)
                pe.wait_ge(gates_ready, l + 1)
                pe.wait_ge(score_copied, 8 * (l + 1))
                for a in range(3):
                    for t in range(TB):
                        o = bank(M[a // 2])[:, SEQ * (a % 2) + P * t:SEQ * (a % 2) + P * (t + 1)]
                        last = turn(o, res[:, a, PH * t:PH * (t + 1), :].rearrange("p a k -> p (a k)"), ident)
                last.then_inc(choice_turned, 1)
                stage(l, B_U + N_U1, N_U - N_U1)

                def gate(b, s):
                    pe.wait_ge(gated, l * N_GATE + b + 1)
                    ge(pe, gate_used, b - 1 + l * N_GATE)
                    for t in range(BATCH):
                        o = bank(M[s]).rearrange("p (i t) -> p t i", t=BATCH)[:, t, :]
                        last = mm(o, onehot[:, s, 0, t, :], onehot[:, s, 1, t, :], start=True, stop=True)
                    last.then_inc(gate_mat, 1)
                pe.wait_ge(choices_ready, l + 1)
                gate(0, 0)
                gate(1, 1)
                with pe.Fori(1, N_GATE // 2) as i:
                    for s in range(2):
                        gate(2 * i + s, s)

                def outputs(i, first=False, end=False):
                    for j in range(RING):
                        n = l * N_BLOCKS + B_V + RING * i + j
                        s = j % 2
                        pe.wait_ge(hi_ready, n + 1)
                        pe.wait_ge(phi_ready, l * N_V + RING * i + j + 1)
                        start, stop = first and j == 0, end and j == RING - 1

                        def part(pp, vv, begin, close):
                            for t in range(TB):
                                for f in range(2):
                                    last = mm(bank(Y[2 * t + f]), pp[:, s, P * t:P * (t + 1)],
                                              vv[:, s, 512 * f:512 * (f + 1)], start=begin, stop=close,
                                              skip_group_check=True)
                            return last
                        part(p_hi, w_hi, start, False)
                        pe.wait_ge(plo_ready, l * N_V + RING * i + j + 1)
                        part(p_lo, w_hi, False, False)
                        pe.wait_ge(lo_ready, n + 1)
                        last = part(p_hi, w_lo, False, stop)
                        last.then_inc(block_done, 1)
                outputs(0, first=True)
                with pe.Fori(1, N_V // RING - 1) as i:
                    outputs(i)
                outputs(N_V // RING - 1, end=True)
                mm(bank(M[0])[0:1, 0:1], ident[:, 0:1], ident[:, 0:1], start=True, stop=True).then_inc(y_done, 1)
                for k in range(KC):
                    pe.wait_ge(y_copied, 4 * (l + 1))
                    if k >= 2:
                        pe.wait_ge(y_used, KC * l + k - 1)
                    for t in range(TB):
                        src = words(W_PJ, 4, 512)[:, 2 * t + k // 4, P * (k % 4):P * (k % 4 + 1)]
                        last = turn(bank(M[k % 2])[:, P * t:P * (t + 1)], src, ident)
                    last.then_inc(y_turned, 1)
            norm(2 * DEPTH)


def constants():
    con = np.zeros((P, K_ALL), np.float32)
    con[:, K_ID:K_ID + P] = np.eye(P)
    con[:, K_ONE:K_ONE + P] = 1
    con[:, K_IOTA:K_IOTA + P] = np.arange(P)
    ret, att = np.zeros((P, P)), np.zeros((P, P))
    for p in range(P):
        base, r = p // 64 * 64, p % 64
        ret[base + (r + 32) % 64, p] = -1 if r < 32 else 1
        if r < 16:
            att[base + (r + 8) % 16, p] = -1 if r < 8 else 1
    con[:, K_PR:K_PR + P], con[:, K_PA:K_PA + P] = ret, att
    f32 = np.float32
    inv_r = np.power(f32(10000.0), -np.arange(32, dtype=f32) * f32(2 / 64))
    inv_a = np.power(f32(500000.0), -np.arange(8, dtype=f32) * f32(2 / 16))
    r = np.arange(P) % 64
    con[:, K_FR] = inv_r[r % 32]
    con[:, K_FA] = np.where(r < 16, inv_a[r % 8], 0)
    con[:, K_EPS] = EPS
    log_g = np.log(1.0 - np.power(2.0, -5.0 - np.arange(RH)))
    diff = np.arange(SEQ)[None, :] - np.arange(P)[:, None]
    full = np.where(diff >= 0, np.exp(log_g[:, None, None] * np.maximum(diff, 0)), 0) * RDK ** -0.5
    decay = np.concatenate([full, full[:, :, :P]], axis=2).transpose(1, 0, 2).astype(np.float32)
    q, k = np.arange(P)[:, None], np.arange(2 * P)[None, :]
    rel = q + P - k
    mask = np.where((rel >= 0) & (rel < P), 0.0, -1e30 / ATT_SCALE).astype(np.float32)
    return con, np.ascontiguousarray(decay.reshape(P, RH * DW)), mask


def kernel(x, c, positions, ada_w, ada_b, norm1_g, norm2_g, w_in, ret_gn_g, sinks, w_out,
           peer_wq, peer_k1, peer_k2, peer_u, peer_v, final_g):
    from concourse import bacc
    from concourse.bass_utils import run_bass_kernel_spmd

    arr = {k: np.asarray(a) for k, a in dict(
        x=x, c=c, positions=positions, ada_w=ada_w, ada_b=ada_b, norm1_g=norm1_g, norm2_g=norm2_g, w_in=w_in,
        ret_gn_g=ret_gn_g, sinks=sinks, w_out=w_out, peer_wq=peer_wq, peer_k1=peer_k1, peer_k2=peer_k2,
        peer_u=peer_u, peer_v=peer_v, final_g=final_g).items()}

    def blocks(w):
        l, d, n = w.shape
        return w.reshape(l, d // P, P, n // P, P).transpose(0, 3, 2, 1, 4).reshape(l, n // P, P, d)

    def cols(a):
        return a.reshape(-1, P).T

    con, decay, mask = constants()
    widths = dict(rq=512, rk=512, rv=1024, rg=1024, aq=1024, ak=256, av=256, ga=1024, gb=1024)
    at, start = {}, 0
    for name, w in widths.items():
        at[name] = np.arange(start, start + w)
        start += w
    heads = [h for a in (0, 8) for j in range(4) for h in (a + j, a + 4 + j)]
    at["aq"] = at["aq"].reshape(AH, AHD)[heads].reshape(-1)
    order = np.concatenate([at[n] for n in ("rq", "rk", "aq", "ak", "rv", "av", "rg", "ga", "gb")])
    keys = np.stack([arr["peer_k1"], arr["peer_k2"]], axis=2)
    u5 = arr["peer_u"].reshape(DEPTH, NKEYS, NKEYS, KC, P)
    vec = np.concatenate([
        cols(arr["norm1_g"]), cols(arr["norm2_g"]), cols(arr["ret_gn_g"]), cols(arr["final_g"]), cols(arr["ada_b"]),
        np.broadcast_to(arr["sinks"].reshape(1, -1), (P, DEPTH * AH))], axis=1)
    ins = {
        "x": arr["x"].reshape(SEQ, KC, P).transpose(2, 1, 0),
        "c": arr["c"].reshape(D),
        "positions": arr["positions"].reshape(SEQ),
        "consts": con, "decay": decay, "mask": mask, "vectors": vec,
        "ada": arr["ada_w"].transpose(0, 2, 1).reshape(DEPTH, N_MOD, P, D),
        "win": blocks(arr["w_in"][:, :, order]),
        "wout": blocks(arr["w_out"]),
        "wq": blocks(arr["peer_wq"]),
        "keys": keys.transpose(0, 4, 1, 2, 3).reshape(DEPTH, P, 2 * PH * NKEYS),
        "u": u5.transpose(0, 2, 4, 3, 1).reshape(DEPTH, NKEYS, P, D),
        "v": arr["peer_v"].reshape(DEPTH, NKEYS, NKEYS, D).transpose(0, 2, 1, 3),
    }
    nc = bacc.Bacc("TRN2", target_bir_lowering=False, num_devices=1)
    arrays, args = {}, []
    for name, a in ins.items():
        a = np.ascontiguousarray(a)
        arrays[f"in_{name}"] = a
        args.append(nc.dram_tensor(f"in_{name}", a.shape, mybir.dt.from_np(a.dtype), kind="ExternalInput").ap())
    out = nc.dram_tensor("out", (P, KC, SEQ), F32, kind="ExternalOutput").ap()
    build(nc, *args, out)
    r = run_bass_kernel_spmd(nc, [arrays], core_ids=[0])
    y = r.results[0]["out"]
    return np.ascontiguousarray(y.transpose(2, 1, 0)).reshape(1, SEQ, D)
```
